# Optimizing a Trainium2 kernel written in Bass

```python
import jax, jax.numpy as jnp
from jax import lax
import numpy as np

D_MODEL = 1024
BATCH = 1
SEQ = 256
DEPTH = 2
DEC_BATCH = 8
DEC_SEQ = 4
PAST_LEN = 256
PAGE_SIZE = 128

HEAD_DIM = 64
N_HEADS_A = D_MODEL // HEAD_DIM
MOBA_BLOCK = 256
MOBA_TOPK = 3
MOBA_QCHUNK = 128
DIL_GROUPS = ((128, 1), (512, 4), (2048, 16))
N_GROUPS_B = len(DIL_GROUPS)
N_HEADS_B = D_MODEL // (2 * HEAD_DIM)
W_MAX = max(w for w, _ in DIL_GROUPS)
ROT_DIM = HEAD_DIM // 4
ROPE_THETA = 500000.0
ATTN_SCALE = HEAD_DIM ** -0.5
D_FF = 2816
N_EXPERTS = 8
TOP_K = 2
D_FF_EXPERT = 3584
MOE_BLOCK = 128
N_A_LAYERS = DEPTH // 2
N_B_LAYERS = DEPTH - N_A_LAYERS
N_DENSE = (DEPTH + 1) // 2
N_MOE = DEPTH // 2
RMS_EPS = 1e-6

kernel_name = 'yoco_moba_dilated_moe_step'

def rmsnorm(x, g):
    xf = x.astype(jnp.float32)
    y = xf * lax.rsqrt(jnp.mean(xf * xf, axis=-1, keepdims=True) + RMS_EPS)
    return (y * g.astype(jnp.float32)).astype(x.dtype)

def rope(x, pos):
    half = ROT_DIM // 2
    inv = ROPE_THETA ** (-2.0 * jnp.arange(half, dtype=jnp.float32) / ROT_DIM)
    ang = pos.astype(jnp.float32)[:, None] * inv[None, :]
    shp = (pos.shape[0],) + (1,) * (x.ndim - 3) + (half,)
    cos = jnp.cos(ang).reshape(shp)
    sin = jnp.sin(ang).reshape(shp)
    xf = x.astype(jnp.float32)
    x1 = xf[..., :half]
    x2 = xf[..., half:ROT_DIM]
    return jnp.concatenate([x1 * cos - x2 * sin, x2 * cos + x1 * sin, xf[..., ROT_DIM:]], axis=-1).astype(x.dtype)

def swiglu(x, w_gu, w_down):
    g, u = jnp.split(x @ w_gu, 2, axis=-1)
    return (jax.nn.silu(g) * u) @ w_down

def moe_ffn(x, w_router, w_gu, w_down):
    n, d = x.shape
    logits = jnp.einsum('nd,de->ne', x, w_router, preferred_element_type=jnp.float32)
    top_val, top_idx = lax.top_k(logits, TOP_K)
    gates = jax.nn.softmax(top_val, axis=-1).astype(x.dtype)
    a = n * TOP_K
    e_flat = top_idx.reshape(-1)
    tok_flat = jnp.arange(a, dtype=jnp.int32) // TOP_K
    order = jnp.argsort(e_flat)
    e_sorted = e_flat[order]
    counts = jnp.bincount(e_flat, length=N_EXPERTS)
    starts = jnp.cumsum(counts) - counts
    padded = (counts + MOE_BLOCK - 1) // MOE_BLOCK * MOE_BLOCK
    pends = jnp.cumsum(padded)
    pstarts = pends - padded
    dest = pstarts[e_sorted] + (jnp.arange(a) - starts[e_sorted])
    n_blocks = -(-a // MOE_BLOCK) + N_EXPERTS
    slot_tok = jnp.full((n_blocks * MOE_BLOCK,), n, jnp.int32).at[dest].set(tok_flat[order])
    block_exp = jnp.clip(jnp.searchsorted(pends, jnp.arange(n_blocks) * MOE_BLOCK, side='right'), 0, N_EXPERTS - 1)
    x_pad = jnp.concatenate([x, jnp.zeros((1, d), x.dtype)], axis=0)

    def run_block(args):
        toks, e = args
        return swiglu(x_pad[toks], w_gu[e], w_down[e])

    out = lax.map(run_block, (slot_tok.reshape(n_blocks, MOE_BLOCK), block_exp)).reshape(-1, d)
    dest_orig = jnp.zeros_like(dest).at[order].set(dest)
    return jnp.sum(out[dest_orig].reshape(n, TOP_K, d) * gates[..., None], axis=1)

def a_qkv(x, pos, norm_g, w_qkv, qn, kn):
    n, t, _ = x.shape
    qkv = (rmsnorm(x, norm_g) @ w_qkv).reshape(n, t, 3, N_HEADS_A, HEAD_DIM)
    q = rope(rmsnorm(qkv[:, :, 0], qn), pos)
    k = rope(rmsnorm(qkv[:, :, 1], kn), pos)
    return q, k, qkv[:, :, 2]

def moba_one(q, k_seq, v_seq, q_start):
    qc, h, dh = q.shape
    nblk = k_seq.shape[0] // MOBA_BLOCK
    kb = k_seq.reshape(nblk, MOBA_BLOCK, h, dh)
    vb = v_seq.reshape(nblk, MOBA_BLOCK, h, dh)
    k_mean = jnp.mean(kb.astype(jnp.float32), axis=1)
    own = q_start // MOBA_BLOCK
    gate = jnp.einsum('qhd,nhd->qhn', q.astype(jnp.float32), k_mean)
    gate = jnp.where((jnp.arange(nblk) < own)[None, None, :], gate, -jnp.inf)
    n_sel = min(MOBA_TOPK, nblk)
    _, sel = lax.top_k(gate, n_sel)
    sel_ok = sel < own
    hid = jnp.arange(h)[None, :, None]
    k_sel = kb.transpose(2, 0, 1, 3)[hid, sel]
    v_sel = vb.transpose(2, 0, 1, 3)[hid, sel]
    s_sel = jnp.einsum('qhd,qhjkd->qhjk', q, k_sel, preferred_element_type=jnp.float32) * ATTN_SCALE
    s_sel = jnp.where(sel_ok[..., None], s_sel, -jnp.inf).reshape(qc, h, n_sel * MOBA_BLOCK)
    k_own = lax.dynamic_slice_in_dim(k_seq, own * MOBA_BLOCK, MOBA_BLOCK, axis=0)
    v_own = lax.dynamic_slice_in_dim(v_seq, own * MOBA_BLOCK, MOBA_BLOCK, axis=0)
    s_own = jnp.einsum('qhd,khd->qhk', q, k_own, preferred_element_type=jnp.float32) * ATTN_SCALE
    kpos = own * MOBA_BLOCK + jnp.arange(MOBA_BLOCK)
    qpos = q_start + jnp.arange(qc)
    s_own = jnp.where((kpos[None, :] <= qpos[:, None])[:, None, :], s_own, -jnp.inf)
    p = jax.nn.softmax(jnp.concatenate([s_sel, s_own], axis=-1), axis=-1).astype(v_seq.dtype)
    n_k = n_sel * MOBA_BLOCK
    o = jnp.einsum('qhk,qhkd->qhd', p[..., :n_k], v_sel.reshape(qc, h, n_k, dh))
    return o + jnp.einsum('qhk,khd->qhd', p[..., n_k:], v_own)

def moba_prompt(q, k, v):
    b, s, h, dh = q.shape
    pad = (-s) % MOBA_BLOCK
    kp = jnp.pad(k, ((0, 0), (0, pad), (0, 0), (0, 0)))
    vp = jnp.pad(v, ((0, 0), (0, pad), (0, 0), (0, 0)))
    qc = min(MOBA_QCHUNK, s)
    nc = s // qc

    def one(i):
        bi = i // nc
        start = (i % nc) * qc
        q_c = lax.dynamic_slice_in_dim(q[bi], start, qc, axis=0)
        return moba_one(q_c, kp[bi], vp[bi], start)

    return lax.map(one, jnp.arange(b * nc)).reshape(b, s, h, dh)

def moba_sample(q, k_new, v_new, pool_k, pool_v, page_table):
    nb, ns, h, dh = q.shape
    past = page_table.shape[1] * pool_k.shape[1]
    pad = (-(past + ns)) % MOBA_BLOCK

    def one(args):
        q_b, kn, vn, pages = args
        kseq = jnp.concatenate([pool_k[pages].reshape(past, h, dh).astype(kn.dtype), kn, jnp.zeros((pad, h, dh), kn.dtype)], axis=0)
        vseq = jnp.concatenate([pool_v[pages].reshape(past, h, dh).astype(vn.dtype), vn, jnp.zeros((pad, h, dh), vn.dtype)], axis=0)
        return moba_one(q_b, kseq, vseq, past)

    return lax.map(one, (q, k_new, v_new, page_table))

def shared_kv(x, pos, norm_g, w_kv, kn):
    n, t, _ = x.shape
    kv = (rmsnorm(x, norm_g) @ w_kv).reshape(n, t, 2, N_HEADS_B, HEAD_DIM)
    return rope(rmsnorm(kv[:, :, 0], kn), pos), kv[:, :, 1]

def b_query(x, pos, norm_g, w_q, qn):
    n, t, _ = x.shape
    q = (rmsnorm(x, norm_g) @ w_q).reshape(n, t, N_GROUPS_B, N_HEADS_B, HEAD_DIM)
    return rope(rmsnorm(q, qn), pos)

def dilated_prompt(q, k, v, dilation, span):
    b, s, h, dh = q.shape
    l = s // dilation
    nb = -(-l // span)
    lp = nb * span

    def strided(x):
        return x.reshape(b, l, dilation, h, dh).transpose(0, 2, 1, 3, 4)

    qs = jnp.pad(strided(q), ((0, 0), (0, 0), (0, lp - l), (0, 0), (0, 0))).reshape(b, dilation, nb, span, h, dh)

    def band(x):
        xp = jnp.pad(strided(x), ((0, 0), (0, 0), (span, lp - l), (0, 0), (0, 0)))
        prev = xp[:, :, :lp].reshape(b, dilation, nb, span, h, dh)
        cur = xp[:, :, span:].reshape(b, dilation, nb, span, h, dh)
        return jnp.concatenate([prev, cur], axis=3)

    kb, vb = band(k), band(v)
    sc = jnp.einsum('bdnqhc,bdnkhc->bdnhqk', qs, kb, preferred_element_type=jnp.float32) * ATTN_SCALE
    qa = jnp.arange(span)[:, None]
    kbi = jnp.arange(2 * span)[None, :]
    dist = qa - kbi + span
    m_k = jnp.arange(nb)[:, None, None] * span + kbi[None] - span
    mask = ((dist >= 0) & (dist <= span))[None] & (m_k >= 0)
    sc = jnp.where(mask[None, None, :, None], sc, -jnp.inf)
    lse = jax.nn.logsumexp(sc, axis=-1)
    p = jnp.exp(sc - lse[..., None]).astype(v.dtype)
    o = jnp.einsum('bdnhqk,bdnkhc->bdnqhc', p, vb)
    o = o.reshape(b, dilation, lp, h, dh)[:, :, :l].transpose(0, 2, 1, 3, 4).reshape(b, s, h, dh)
    lse = lse.transpose(0, 1, 2, 4, 3).reshape(b, dilation, lp, h)[:, :, :l].transpose(0, 2, 1, 3).reshape(b, s, h)
    return o, lse

def dilated_sample(q, k_ctx, v_ctx, dilation, span):
    qn = q.shape[1]
    w_buf = k_ctx.shape[1] - qn
    idx = w_buf + jnp.arange(qn)[:, None] - jnp.arange(span + 1)[None, :] * dilation
    valid = idx >= 0
    idxc = jnp.maximum(idx, 0)
    ks = k_ctx[:, idxc]
    vs = v_ctx[:, idxc]
    sc = jnp.einsum('nqhc,nqjhc->nqhj', q, ks, preferred_element_type=jnp.float32) * ATTN_SCALE
    sc = jnp.where(valid[None, :, None, :], sc, -jnp.inf)
    lse = jax.nn.logsumexp(sc, axis=-1)
    p = jnp.exp(sc - lse[..., None]).astype(v_ctx.dtype)
    return jnp.einsum('nqhj,nqjhc->nqhc', p, vs), lse

def merge_groups(outs, lses):
    w = jax.nn.softmax(jnp.stack(lses, axis=0), axis=0)
    o = jnp.sum(w[..., None] * jnp.stack(outs, axis=0).astype(jnp.float32), axis=0)
    return o.astype(outs[0].dtype)

def setup_inputs(seed: int = 0) -> dict:
    key = jax.random.key(seed)
    ks = jax.random.split(key, 32)
    n_pages = PAST_LEN // PAGE_SIZE
    n_used = DEC_BATCH * n_pages
    n_phys = n_used + n_used // 4
    w_buf = min(W_MAX, PAST_LEN)

    def nrm(k, shape, scale=1.0):
        return jax.random.normal(k, shape, jnp.float32) * scale

    def gain(k, shape):
        return 1.0 + 0.1 * jax.random.normal(k, shape, jnp.float32)

    return {
        'x_prompt': nrm(ks[0], (BATCH, SEQ, D_MODEL)),
        'x_sample': nrm(ks[1], (DEC_BATCH, DEC_SEQ, D_MODEL)),
        'cache_a_k': nrm(ks[2], (N_A_LAYERS, n_phys, PAGE_SIZE, N_HEADS_A, HEAD_DIM)),
        'cache_a_v': nrm(ks[3], (N_A_LAYERS, n_phys, PAGE_SIZE, N_HEADS_A, HEAD_DIM)),
        'cache_b_k': nrm(ks[4], (DEC_BATCH, w_buf, N_HEADS_B, HEAD_DIM)),
        'cache_b_v': nrm(ks[5], (DEC_BATCH, w_buf, N_HEADS_B, HEAD_DIM)),
        'page_table': jax.random.permutation(ks[6], n_phys)[:n_used].reshape(DEC_BATCH, n_pages).astype(jnp.int32),
        'norm_attn_a': gain(ks[7], (N_A_LAYERS, D_MODEL)),
        'w_qkv_a': nrm(ks[8], (N_A_LAYERS, D_MODEL, 3 * N_HEADS_A * HEAD_DIM), D_MODEL ** -0.5),
        'qnorm_a': gain(ks[9], (N_A_LAYERS, HEAD_DIM)),
        'knorm_a': gain(ks[10], (N_A_LAYERS, HEAD_DIM)),
        'w_o_a': nrm(ks[11], (N_A_LAYERS, N_HEADS_A * HEAD_DIM, D_MODEL), (N_HEADS_A * HEAD_DIM) ** -0.5),
        'norm_kv_b': gain(ks[12], (D_MODEL,)),
        'w_kv_b': nrm(ks[13], (D_MODEL, 2 * N_HEADS_B * HEAD_DIM), D_MODEL ** -0.5),
        'knorm_b': gain(ks[14], (HEAD_DIM,)),
        'norm_attn_b': gain(ks[15], (N_B_LAYERS, D_MODEL)),
        'w_q_b': nrm(ks[16], (N_B_LAYERS, D_MODEL, N_GROUPS_B * N_HEADS_B * HEAD_DIM), D_MODEL ** -0.5),
        'qnorm_b': gain(ks[17], (N_B_LAYERS, HEAD_DIM)),
        'w_o_b': nrm(ks[18], (N_B_LAYERS, N_HEADS_B * HEAD_DIM, D_MODEL), (N_HEADS_B * HEAD_DIM) ** -0.5),
        'norm_ffn': gain(ks[19], (DEPTH, D_MODEL)),
        'w_gu_dense': nrm(ks[20], (N_DENSE, D_MODEL, 2 * D_FF), D_MODEL ** -0.5),
        'w_down_dense': nrm(ks[21], (N_DENSE, D_FF, D_MODEL), D_FF ** -0.5),
        'w_router': nrm(ks[22], (N_MOE, D_MODEL, N_EXPERTS), D_MODEL ** -0.5),
        'w_gu_moe': nrm(ks[23], (N_MOE, N_EXPERTS, D_MODEL, 2 * D_FF_EXPERT), D_MODEL ** -0.5),
        'w_down_moe': nrm(ks[24], (N_MOE, N_EXPERTS, D_FF_EXPERT, D_MODEL), D_FF_EXPERT ** -0.5),
    }

def reference(x_prompt, x_sample, cache_a_k, cache_a_v, cache_b_k, cache_b_v, page_table,
              norm_attn_a, w_qkv_a, qnorm_a, knorm_a, w_o_a,
              norm_kv_b, w_kv_b, knorm_b, norm_attn_b, w_q_b, qnorm_b, w_o_b,
              norm_ffn, w_gu_dense, w_down_dense, w_router, w_gu_moe, w_down_moe):
    b, s, d = x_prompt.shape
    nb, ns, _ = x_sample.shape
    past = page_table.shape[1] * cache_a_k.shape[2]
    pos_p = jnp.arange(s)
    pos_s = past + jnp.arange(ns)
    xp, xs = x_prompt, x_sample
    ak_p, av_p, ak_s, av_s = [], [], [], []
    for l in range(DEPTH):
        if l < N_A_LAYERS:
            qp, kp, vp = a_qkv(xp, pos_p, norm_attn_a[l], w_qkv_a[l], qnorm_a[l], knorm_a[l])
            qs, ks_, vs_ = a_qkv(xs, pos_s, norm_attn_a[l], w_qkv_a[l], qnorm_a[l], knorm_a[l])
            op = moba_prompt(qp, kp, vp)
            os_ = moba_sample(qs, ks_, vs_, cache_a_k[l], cache_a_v[l], page_table)
            xp = xp + op.reshape(b, s, -1) @ w_o_a[l]
            xs = xs + os_.reshape(nb, ns, -1) @ w_o_a[l]
            ak_p.append(kp)
            av_p.append(vp)
            ak_s.append(ks_)
            av_s.append(vs_)
        else:
            j = l - N_A_LAYERS
            qp = b_query(xp, pos_p, norm_attn_b[j], w_q_b[j], qnorm_b[j])
            qs = b_query(xs, pos_s, norm_attn_b[j], w_q_b[j], qnorm_b[j])
            outs_p, lses_p, outs_s, lses_s = [], [], [], []
            for g, (win, dil) in enumerate(DIL_GROUPS):
                o_g, l_g = dilated_prompt(qp[:, :, g], kb_p, vb_p, dil, win // dil)
                outs_p.append(o_g)
                lses_p.append(l_g)
                o_g, l_g = dilated_sample(qs[:, :, g], k_ctx, v_ctx, dil, win // dil)
                outs_s.append(o_g)
                lses_s.append(l_g)
            xp = xp + merge_groups(outs_p, lses_p).reshape(b, s, -1) @ w_o_b[j]
            xs = xs + merge_groups(outs_s, lses_s).reshape(nb, ns, -1) @ w_o_b[j]
        tok = jnp.concatenate([xp.reshape(-1, d), xs.reshape(-1, d)], axis=0)
        h = rmsnorm(tok, norm_ffn[l])
        if l % 2 == 0:
            f = swiglu(h, w_gu_dense[l // 2], w_down_dense[l // 2])
        else:
            f = moe_ffn(h, w_router[l // 2], w_gu_moe[l // 2], w_down_moe[l // 2])
        tok = tok + f
        xp = tok[:b * s].reshape(b, s, d)
        xs = tok[b * s:].reshape(nb, ns, d)
        if l == N_A_LAYERS - 1:
            kb_p, vb_p = shared_kv(xp, pos_p, norm_kv_b, w_kv_b, knorm_b)
            kb_s, vb_s = shared_kv(xs, pos_s, norm_kv_b, w_kv_b, knorm_b)
            k_ctx = jnp.concatenate([cache_b_k.astype(kb_s.dtype), kb_s], axis=1)
            v_ctx = jnp.concatenate([cache_b_v.astype(vb_s.dtype), vb_s], axis=1)
    keep = min(W_MAX, s)
    a_k_prompt = jnp.stack(ak_p, axis=0)
    a_v_prompt = jnp.stack(av_p, axis=0)
    a_k_sample = jnp.stack(ak_s, axis=0)
    a_v_sample = jnp.stack(av_s, axis=0)
    b_k_prompt = kb_p[:, s - keep:]
    b_v_prompt = vb_p[:, s - keep:]
    return (xp, xs, a_k_prompt, a_v_prompt, b_k_prompt, b_v_prompt, a_k_sample, a_v_sample, kb_s, vb_s)


_drawn_inputs = setup_inputs


def setup_inputs(seed=0):
    import zlib

    import numpy as np

    out = dict(_drawn_inputs(seed))
    spreads = {}
    factors = {}
    for name, (base, spread) in spreads.items():
        noise = np.random.default_rng([zlib.crc32(name.encode()), seed]).standard_normal(out[name].shape)
        drawn = base * np.exp(spread * noise) if base else spread * noise
        out[name] = __import__('jax').numpy.asarray(drawn.astype(out[name].dtype))
    for name, factor in factors.items():
        out[name] = (out[name] * factor).astype(out[name].dtype)
    return out
```

```python
import concourse.bass as bass
from concourse import mybir
from contextlib import ExitStack

F32 = mybir.dt.float32
F32R = mybir.dt.float32r
I32 = mybir.dt.int32
ALU = mybir.AluOpType
ACT = mybir.ActivationFunctionType
AXX = mybir.AxisListType.X
AXXY = mybir.AxisListType.XY

P = 128
D = 1024
KD = D // P
SEQ = 256
NSEQ, QLEN = 8, 4
NSAMP = NSEQ * QLEN
T = SEQ + NSAMP
PAST = 256
PAGE = 128
NPHYS = 20
DH = 64
HA, HB, GB = 16, 8, 3
FF = 2816
KF = FF // P
NE = 8
FE = 3584
KE = FE // P
NBLK = 4
SCALE = DH ** -0.5
EPS = 1e-6
NEG = -1e30
TB = [(0, P), (P, P), (2 * P, NSAMP)]

PIECE = 2048
RAW = 6
SPL = 3
QKV_P, WO_P, GU_P, DN_P, KV_P, QB_P, WOB_P = 12, 4, 22, 16, 4, 6, 2
PRE = QKV_P + WO_P + GU_P + DN_P + KV_P + QB_P + WOB_P
EXP_GU, EXP_DN = 28, 14
PER = EXP_GU + EXP_DN

CONST = {}
_at = 0
for _name, _n in (("ident", P), ("headsum", P), ("featsum", P), ("rot", P), ("cos", T), ("sin", T), ("before", P),
                  ("ones", P), ("slots", P), ("pick", NSAMP), ("expert", NE * 3), ("over", 2 * NE * 2),
                  ("g_attn_a", KD), ("g_ffn0", KD), ("g_kv", KD), ("g_attn_b", KD), ("g_ffn1", KD),
                  ("qn_a", 1), ("kn_a", 1), ("qn_b", 1), ("kn_b", 1), ("eps", 1)):
    CONST[_name] = (_at, _at + _n)
    _at += _n
NCONST = _at
MASK_A = 384 + NSAMP * NSEQ
REGION = 96256
MASK_B = GB * 384 + PAST + NSAMP * NSEQ


def build_program(nc, io):
    ctx = ExitStack()
    with ctx:
        def sb(name, shape, dt=F32):
            return ctx.enter_context(nc.sbuf_tensor(name, shape, dt))

        named = {}

        def sem(name):
            if name not in named:
                named[name] = ctx.enter_context(nc.semaphore(name))
            return named[name]

        raw = sb("raw", [P, RAW, PIECE])
        whi = sb("whi", [P, SPL, PIECE], F32R)
        wlo = sb("wlo", [P, SPL, PIECE], F32R)
        cst = sb("cst", [P, NCONST])
        xT = sb("xT", [P, KD, T])
        sb("region", [P, REGION // 4])
        base = nc.sbuf_base - REGION

        def at(name, off, shape, dt=F32):
            size = 4
            for s in shape[1:]:
                size *= s
            assert off + size <= REGION, name
            return nc.alloc_sbuf_tensor_at(name, shape, dt, offset=base + off)

        def con(name, rows=P):
            a, b = CONST[name]
            return cst[0:rows, a:b]

        hh = at("hh", 30720, [P, KD, T], F32R)
        hl = at("hl", 39936, [P, KD, T], F32R)
        sq = at("sq", 49152, [P, KD, T])
        hn = at("hn", 58368, [P, KD, T])
        rt = at("rt", 25344, [P, 2, T])
        rs = at("rs", 27648, [P, 2, T])
        hh2 = at("hh2", 67584, [P, KD, T], F32R)
        hl2 = at("hl2", 76800, [P, KD, T], F32R)
        gh = at("gh", 0, [P, KF, T], F32R)
        gl = at("gl", 67584, [P, KF, T], F32R)
        gate_s = at("gate_s", 58368, [P, 4, T])
        gate_u = at("gate_u", 62976, [P, 4, T])

        def attention(tag, nh, ng, nmask, off):
            b = dict(tag=tag, nh=nh, ng=ng, nj=nh // 2, nq=ng * nh // 2, hq=nh * QLEN, rows=ng * nh * QLEN, w=nh * DH)
            b["qT"] = at(f"qT_{tag}", off["q"], [P, b["nq"], T])
            b["kT"] = at(f"kT_{tag}", off["k"], [P, b["nj"], T])
            b["vtok"] = at(f"vtok_{tag}", off["v"], [P, 3, b["w"]])
            b["vT"] = at(f"vT_{tag}", off["vT"], [P, b["nj"], T])
            b["ktok"] = at(f"ktok_{tag}", off["ktok"], [P, 3, b["w"]])
            b["oT"] = at(f"oT_{tag}", off["o"], [P, b["nj"], T])
            b["mask"] = at(f"mask_{tag}", off["mask"], [P, nmask])
            b["kraw"] = at(f"kraw_{tag}", off["kraw"], [P, 2, b["w"]])
            b["vraw"] = at(f"vraw_{tag}", off["vraw"], [P, 2, 2, b["w"]])
            b["keys"] = at(f"keys_{tag}", off["keys"], [P, b["nj"], PAST + NSAMP])
            b["qblk"] = at(f"qblk_{tag}", off["qblk"], [P, 2, b["nj"], b["rows"]])
            b["s"] = at(f"s_{tag}", off["s"], [P, 2, ng, 384])
            b["p"] = at(f"p_{tag}", off["p"], [P, 2, ng, 384])
            b["pt"] = at(f"pt_{tag}", off["pt"], [P, 2, 384])
            b["ss"] = at(f"ss_{tag}", off["ss"], [b["rows"], 2, PAST + NSAMP])
            b["sp"] = at(f"sp_{tag}", off["sp"], [b["rows"], 2, PAST + NSAMP])
            b["spt"] = at(f"spt_{tag}", off["spt"], [P, 2, 3, b["hq"]])
            b["st"] = sb(f"st_{tag}", [P, 2, 12])
            b["sst"] = sb(f"sst_{tag}", [b["rows"], 2, 12])
            return b

        A = attention("a", HA, 1, MASK_A, dict(
            q=0, k=9216, v=18432, vT=58368, ktok=30720, kraw=67584, vraw=75776, mask=92160,
            keys=30720, s=39936, p=43008, pt=46080, o=49152, qblk=58368, ss=62464, sp=64768, spt=94720))
        B = attention("b", HB, GB, MASK_B, dict(
            q=0, k=13824, v=18432, vT=62976, ktok=46848, kraw=25344, vraw=86016, mask=57856,
            keys=30720, pt=35328, ss=38400, sp=40704, spt=43008, qblk=43776, s=67584, p=76800, o=53248))
        A["pieces"], A["nrot"], A["nv"] = 0, 16, 8
        B["pieces"], B["nrot"], B["nv"] = QKV_P + WO_P + GU_P + DN_P, 16, 4

        xtok = at("xtok", 0, [P, 3, D])
        htok = at("htok", 12288, [P, 3, D])
        pm = at("pm", 24576, [P, 3, P])
        pmt = at("pmt", 30208, [P, 3, P], F32R)
        acth = at("acth", 36864, [P, KE, P], F32R)
        actl = at("actl", 51200, [P, KE, P], F32R)
        xgh = at("xgh", 65536, [P, KD, P], F32R)
        xgl = at("xgl", 69632, [P, KD, P], F32R)
        oe = at("oe", 73728, [P, D])
        oh = at("oh", 77824, [P, D], F32R)
        ol = at("ol", 81920, [P, D], F32R)
        sg = at("sg", 86016, [P, 512])
        am = at("am", 88064, [P, 512])
        rw = at("rw", 90112, [P, KD, NE])
        rwg = at("rwg", 90368, [P, KD, NE])
        grow = at("grow", 26112, [P, D])
        scratch = at("scratch", 31744, [P, 16])
        sel = at("sel", 90624, [P, 12, 3 * NE])
        pslot = at("pslot", 91776, [P, 3, 13])
        gslot = at("gslot", 91936, [P, 3, 13])
        pcur = at("pcur", 92096, [P, 3])
        gcur = at("gcur", 92128, [P, 2, 3])
        gsl = at("gsl", 92160, [P, 2])
        mst = at("mst", 92192, [P, 3, 8])
        ovf = at("ovf", 92288, [P, 12, 2 * NE])
        tabf = at("tabf", 93056, [P, 16])
        tab = at("tab", 93120, [P, 16], I32)
        pgt = sb("pgt", [1, 2 * NSEQ], I32)

        ps = [ctx.enter_context(nc.psum_tensor(f"bank{i}", [P, 512], F32)) for i in range(8)]

        def cols(w, lo, n):
            return w[:, lo:lo + n].rearrange("(k p) n -> p k n", p=P)

        W = []
        W += [cols(io["w_qkv_a"][0], 256 * i, 256) for i in range(QKV_P)]
        W += [cols(io["w_o_a"][0], 256 * i, 256) for i in range(WO_P)]
        for i in range(GU_P // 2):
            W += [cols(io["w_gu_dense"][0], o + 256 * i, 256) for o in (0, FF)]
        for i in range(DN_P):
            W += [cols(io["w_down_dense"][0][1408 * (i % 2):1408 * (i % 2 + 1), :], P * (i // 2), P)]
        W += [cols(io["w_kv_b"], 256 * i, 256) for i in range(2)]
        W += [cols(io["w_q_b"][0], 256 * i, 256) for i in range(QB_P)]
        W += [cols(io["w_kv_b"], 512 + 256 * i, 256) for i in range(2)]
        W += [cols(io["w_o_b"][0], 512 * i, 512) for i in range(WOB_P)]
        assert len(W) == PRE and PRE % RAW == 0 and PRE % SPL == 0 and PER % RAW == 0 and PER % SPL == 0

        raw_loaded = [sem(f"raw_loaded{i}") for i in range(RAW)]
        hi_ready, pieces_split, pieces_used = sem("hi_ready"), sem("pieces_split"), sem("pieces_used")
        tile_done = sem("tile_done")

        def raw_view(p, a, n):
            return raw[:, p % RAW, 0:a * n].rearrange("p (k n) -> p k n", n=n)

        def load_piece(eng, n, p, src):
            if p >= RAW:
                eng.wait_ge(pieces_split, PER * n + p - RAW + 1)
            eng.dma_start(raw_view(p, src.shape[1], src.shape[2]), src).then_inc(raw_loaded[p % RAW], 16)

        def split_hi(eng, n, p, size=PIECE):
            eng.wait_ge(raw_loaded[p % RAW], 16 * (PER // RAW) * n + 16 * (p // RAW + 1))
            if p >= SPL:
                eng.wait_ge(pieces_used, PER * n + p - SPL + 1)
            nc.scalar.activation(whi[:, p % SPL, 0:size], raw[:, p % RAW, 0:size], ACT.Copy).then_inc(hi_ready, 1)

        def split_lo(eng, n, p, size=PIECE):
            eng.wait_ge(hi_ready, PER * n + p + 1)
            nc.vector.tensor_tensor(wlo[:, p % SPL, 0:size], raw[:, p % RAW, 0:size],
                                    whi[:, p % SPL, 0:size].bitcast(F32), ALU.subtract).then_inc(pieces_split, 1)

        def three(out, lh, ll, rh, rl, start, stop):
            nc.tensor.matmul(out, lh, rh, start=start, stop=False)
            nc.tensor.matmul(out, lh, rl, start=False, stop=False)
            return nc.tensor.matmul(out, ll, rh, start=False, stop=stop)

        def tile_sem(tiles, m):
            return pieces_used if m % tiles[1] == tiles[1] - 1 else tile_done

        def tile_count(tiles, m):
            p0, per, tiles0 = tiles
            if m % per == per - 1:
                return p0 + m // per + 1
            return tiles0 + (m // per) * (per - 1) + m % per + 1

        P_WO = QKV_P
        P_GU = P_WO + WO_P
        P_DN = P_GU + GU_P
        P_WOB = PRE - WOB_P
        tiles_a = (0, 2, 0)
        tiles_wo = (P_WO, 2, 12)
        tiles_gu = (P_GU, 2, 16)
        tiles_b = (B["pieces"], 2, 38)
        tiles_wob = (P_WOB, 4, 48)

        block = ctx.enter_context(nc.Block())

        def gain(name, k):
            a, _ = CONST[name]
            return cst[:, a + k:a + k + 1]

        @block.sync
        def _(eng):
            eng.dma_start(cst[:, :], io["const"]).then_inc(sem("const_loaded"), 16)
            eng.dma_start(xT[:, :, :], io["xT"]).then_inc(sem("x_loaded"), 16)
            for p in range(RAW):
                load_piece(eng, 0, p, W[p])
            eng.dma_start(A["mask"][:, :], io["mask_a"]).then_inc(sem("mask_loaded_a"), 16)
            for p in range(RAW, PRE):
                load_piece(eng, 0, p, W[p])

            def expert_piece(e, q):
                gu = io["w_gu_moe"][0][bass.ds(e, 1), :, :]
                dn = io["w_down_moe"][0][bass.ds(e, 1), :, :]
                if q < EXP_GU:
                    c, part, half = q // 4, q % 4 // 2, q % 2
                    lo = FE * part + 512 * c
                    return gu[:, 512 * half:512 * (half + 1), lo:lo + 512].rearrange("e (k p) n -> p (e k) n", p=P)
                q -= EXP_GU
                return dn[:, 256 * q:256 * (q + 1), :].rearrange("e (k p) n -> p (e k) n", p=P)

            for q in range(2):
                load_piece(eng, 0, PRE + q, expert_piece(0, q))

            def expert_loads(n, e, e_next):
                for q in range(2, PER + 2):
                    src = expert_piece(e, q) if q < PER else expert_piece(e_next, q - PER)
                    load_piece(eng, n, PRE + q, src)

            with eng.Fori(0, NE - 1) as n:
                expert_loads(n, n, n + 1)
            eng.wait_ge(sem("table_ready"), 1)
            over = eng.value_load(tab[0:1, 12:13], min_val=0, max_val=4)
            e8 = eng.value_load(tab[0:1, 8:9], min_val=0, max_val=NE - 1)
            expert_loads(NE - 1, NE - 1, e8)
            with eng.Fori(0, 4) as t:
                with eng.If(t < over):
                    e = eng.value_load(tab[0:1, bass.ds(t + 8, 1)], min_val=0, max_val=NE - 1)
                    e_next = eng.value_load(tab[0:1, bass.ds(t + 9, 1)], min_val=0, max_val=NE - 1)
                    expert_loads(t + NE, e, e_next)
            eng.wait_ge(sem("y_ready"), 1)
            eng.dma_start(io["y"][0:SEQ, :].rearrange("(b p) n -> p b n", p=P), xtok[:, 0:2, :]).then_inc(sem("y_stored"), 16)
            eng.dma_start(io["y"][SEQ:T, :], xtok[0:NSAMP, 2, :]).then_inc(sem("y_stored"), 16)
            eng.wait_ge(sem("y_stored"), 32)

        @block.gpsimd
        def _(eng):
            eng.dma_start(pgt[0:1, :], io["page_table"]).then_inc(sem("pages_loaded"), 16)
            eng.wait_ge(sem("pages_loaded"), 16)

            def store(b, key, val):
                eng.wait_ge(sem(f"tok_done_{b['tag']}"), 2 * b["nj"])
                for buf, out in ((b["ktok"], key), (b["vtok"], val)):
                    eng.dma_start(out[0:SEQ, :].rearrange("(b p) n -> p b n", p=P), buf[:, 0:2, :]).then_inc(sem(f"kv_stored_{b['tag']}"), 16)
                    eng.dma_start(out[SEQ:T, :], buf[0:NSAMP, 2, :]).then_inc(sem(f"kv_stored_{b['tag']}"), 16)

            def caches(b, q, kt, vt):
                if q >= 1:
                    eng.wait_ge(sem(f"ktr_done_{b['tag']}"), q * b["nj"] // 2)
                kt(q)
                if q >= 2:
                    eng.wait_ge(sem(f"spv_done_{b['tag']}"), q - 1)
                vt(q)

            def paged(src, buf, q, done):
                for j in range(2):
                    pg = eng.value_load(pgt[0:1, 2 * q + j:2 * q + j + 1], min_val=0, max_val=NPHYS - 1)
                    eng.dma_start(buf[:, j, :], src[0][bass.ds(pg, 1), :, :].rearrange("a p n -> p (a n)")).then_inc(done, 16)

            def keys_a(q):
                paged(io["cache_a_k"], A["kraw"], q, sem("kraw_loaded_a"))

            def vals_a(q):
                paged(io["cache_a_v"], A["vraw"][:, q % 2], q, sem(f"vraw_loaded_a{q % 2}"))

            caches(A, 0, keys_a, vals_a)
            store(A, io["ak"], io["av"])
            for q in range(1, NSEQ):
                caches(A, q, keys_a, vals_a)

            def window(src, buf, q, done):
                eng.dma_start(buf, src[q].rearrange("(j p) n -> p j n", p=P)).then_inc(done, 16)

            def keys_b(q):
                window(io["cache_b_k"], B["kraw"][:, :, :], q, sem("kraw_loaded_b"))

            def vals_b(q):
                window(io["cache_b_v"], B["vraw"][:, q % 2], q, sem(f"vraw_loaded_b{q % 2}"))

            store(B, io["bk"], io["bv"])
            eng.dma_start(B["mask"][:, :], io["mask_b"]).then_inc(sem("mask_loaded_b"), 16)
            for q in range(NSEQ):
                caches(B, q, keys_b, vals_b)
            eng.wait_ge(sem("o_split_b"), 1)
            eng.dma_start(rw[:, :, :], io["w_router"][0].rearrange("(k p) e -> p k e", p=P)).then_inc(sem("router_loaded"), 16)
            eng.dma_start(grow[:, :], io["g_rows"]).then_inc(sem("router_loaded"), 16)
            for b in "ab":
                eng.wait_ge(sem(f"kv_stored_{b}"), 64)

        @block.tensor
        def _(eng):
            eng.wait_ge(sem("const_loaded"), 16)

            def take(n, p):
                eng.wait_ge(pieces_split, PER * n + p + 1)

            def norm_sum(tag, k):
                eng.wait_ge(sem(f"squared_{tag}"), k + 1)
                ins = nc.tensor.matmul(ps[7][:, 0:T], con("featsum"), sq[:, k], start=k == 0, stop=k == KD - 1)
                if k == KD - 1:
                    ins.then_inc(sem(f"summed_{tag}"), 1)

            def project(b, tiles, sources):
                nrot, nt = b["nrot"], b["nrot"] + b["nv"]
                fresh = set()
                for m in range(nt):
                    if m % 2 == 0:
                        take(0, b["pieces"] + m // 2)
                    if m >= 4:
                        if m - 4 < nrot:
                            eng.wait_ge(sem(f"scaled_{b['tag']}"), m - 3)
                        else:
                            eng.wait_ge(sem(f"v_copied_{b['tag']}"), m - 4 - nrot + 1)
                    name, xh, xl = sources(m)
                    piece = b["pieces"] + m // 2
                    for k in range(KD):
                        if name not in fresh:
                            eng.wait_ge(sem(f"lo_ready_{name}"), k + 1)
                        c = (k * 2 + m % 2) * P
                        ins = three(ps[m % 4][:, 0:T], whi[:, piece % SPL, c:c + P], wlo[:, piece % SPL, c:c + P],
                                    xh[:, k], xl[:, k], k == 0, k == KD - 1)
                    fresh.add(name)
                    ins.then_inc(tile_sem(tiles, m), 1)
                    if 0 <= m - 1 < nrot:
                        r = m - 1
                        eng.wait_ge(sem(f"tile_squared_{b['tag']}"), r + 1)
                        if r >= 2:
                            eng.wait_ge(sem(f"rooted_{b['tag']}"), r - 1)
                        nc.tensor.matmul(ps[4 + r % 2][:, 0:T], con("headsum"), sq[:, r % 2], start=True, stop=True)\
                            .then_inc(sem(f"head_summed_{b['tag']}"), 1)
                    if 0 <= m - 2 < nrot:
                        r = m - 2
                        eng.wait_ge(sem(f"scaled_{b['tag']}"), r + 1)
                        if r >= 2:
                            eng.wait_ge(sem(f"rotated_{b['tag']}"), r - 1)
                        nc.tensor.matmul(ps[6 + r % 2][:, 0:T], con("rot"), sq[:, 2 + r % 2], start=True, stop=True)\
                            .then_inc(sem(f"turned_{b['tag']}"), 1)

            def to_tokens(b):
                for i in range(2 * b["nj"]):
                    src = b["kT"] if i < b["nj"] else b["vT"]
                    j = i % b["nj"]
                    if i == 0:
                        eng.wait_ge(sem(f"rotated_{b['tag']}"), b["nrot"])
                        eng.wait_ge(sem(f"v_copied_{b['tag']}"), b["nv"])
                    if i >= 4:
                        eng.wait_ge(sem(f"tok_done_{b['tag']}"), i - 3)
                    for t0, n in TB:
                        ins = nc.tensor.transpose(ps[i % 4][0:n, t0:t0 + P], src[:, j, t0:t0 + n], con("ident"))
                    ins.then_inc(sem(f"tok_turned_{b['tag']}"), 1)

            def prompt(b):
                tg = b["tag"]
                for h in range(b["nh"] + 3):
                    if h < b["nh"]:
                        r, j = 64 * (h % 2), h // 2
                        if h >= 2:
                            eng.wait_ge(sem(f"masked_{tg}"), h - 1)
                        elif h == 0:
                            eng.wait_ge(sem(f"tok_done_{tg}"), 2 * b["nj"])
                        for g in range(b["ng"]):
                            bank = ps[(h % 2) * b["ng"] + g]
                            q = b["qT"][r:r + 64, g * b["nj"] + j, :]
                            nc.tensor.matmul(bank[:, 0:P], q[:, 0:P], b["kT"][r:r + 64, j, 0:P], start=True, stop=True)
                            ins = nc.tensor.matmul(bank[:, P:384], q[:, P:2 * P], b["kT"][r:r + 64, j, 0:2 * P], start=True, stop=True)
                        ins.then_inc(sem(f"scored_{tg}"), 1)
                    if 0 <= h - 2 < b["nh"]:
                        i = h - 2
                        eng.wait_ge(sem(f"probs_{tg}"), i + 1)
                        if i >= 1:
                            eng.wait_ge(sem(f"pt_copied_{tg}"), i)
                        for c in range(3):
                            ins = nc.tensor.transpose(ps[6][:, c * P:(c + 1) * P], b["p"][:, i % 2, 0, c * P:(c + 1) * P], con("ident"))
                        ins.then_inc(sem(f"pt_turned_{tg}"), 1)
                    if 0 <= h - 3:
                        i = h - 3
                        r = 64 * (i % 2)
                        eng.wait_ge(sem(f"pt_copied_{tg}"), i + 1)
                        if i % 2 == 0 and i >= 2:
                            eng.wait_ge(sem(f"o_copied_{tg}"), i // 2)
                        nc.tensor.matmul(ps[7][r:r + 64, 0:2 * P], b["vtok"][:, 0, i * DH:(i + 1) * DH], b["pt"][:, i % 2, 0:2 * P],
                                         start=True, stop=False)
                        nc.tensor.matmul(ps[7][r:r + 64, P:2 * P], b["vtok"][:, 1, i * DH:(i + 1) * DH], b["pt"][:, i % 2, 2 * P:3 * P],
                                         start=False, stop=True).then_inc(sem(f"pv_done_{tg}"), 1)

            def sample(b, mat):
                tg, half = b["tag"], b["nj"] // 2
                for q in range(NSEQ + 2):
                    if 0 <= q - 1 < NSEQ:
                        i = q - 1
                        for who in range(2):
                            eng.wait_ge(sem(f"keys_copied{who}_{tg}"), half // 2 * (i + 1))
                        eng.wait_ge(sem(f"qblk_{tg}"), i + 1)
                        if i >= 2:
                            eng.wait_ge(sem(f"smasked_{tg}"), i - 1)
                        for j in range(b["nj"]):
                            ins = nc.tensor.matmul(ps[4 + i % 2][0:b["rows"], 0:T], b["qblk"][:, i % 2, j, :], b["keys"][:, j, :],
                                                   start=j == 0, stop=j == b["nj"] - 1)
                        ins.then_inc(sem(f"sscored_{tg}"), 1)
                    if q < NSEQ:
                        eng.wait_ge(sem(f"kraw_loaded_{tg}"), (32 if b is A else 16) * (q + 1))
                        for c in range(half):
                            n = q * half + c
                            if n >= 4:
                                eng.wait_ge(sem(f"keys_copied{n % 2}_{tg}"), (n - 4) // 2 + 1)
                            elif n == 0:
                                eng.wait_ge(sem(f"masked_{tg}"), b["nh"])
                            for u in range(4):
                                j, pg = 2 * c + u // 2, u % 2
                                ins = nc.tensor.transpose(ps[n % 4][:, u * P:(u + 1) * P], b["kraw"][:, pg, j * P:(j + 1) * P], con("ident"))
                            ins.then_inc(sem(f"ktr_done_{tg}"), 1)
                    if 0 <= q - 2:
                        i = q - 2
                        eng.wait_ge(sem(f"sprobs_{tg}"), i + 1)
                        if i >= 1:
                            eng.wait_ge(sem(f"spt_copied_{tg}"), i)
                        else:
                            eng.wait_ge(sem(f"pt_copied_{tg}"), b["nh"])
                        for c, (t0, n) in enumerate(TB):
                            ins = nc.tensor.matmul(ps[6][0:n, c * b["hq"]:(c + 1) * b["hq"]], b["sp"][:, i % 2, t0:t0 + n], mat,
                                                   start=True, stop=True)
                        ins.then_inc(sem(f"spt_turned_{tg}"), 1)
                        eng.wait_ge(sem(f"spt_copied_{tg}"), i + 1)
                        eng.wait_ge(sem(f"vraw_loaded_{tg}{i % 2}"), (32 if b is A else 16) * (i // 2 + 1))
                        if i >= 1:
                            eng.wait_ge(sem(f"so_copied_{tg}"), i)
                        else:
                            eng.wait_ge(sem(f"o_copied_{tg}"), b["nh"] // 2)
                        for j in range(b["nj"]):
                            out = ps[7][:, 8 * j:8 * j + 8]
                            for c in range(2):
                                nc.tensor.matmul(out, b["vraw"][:, i % 2, c, j * P:(j + 1) * P], b["spt"][:, i % 2, c, 8 * j:8 * j + 8],
                                                 start=c == 0, stop=False)
                            ins = nc.tensor.matmul(out, b["vtok"][0:NSAMP, 2, j * P:(j + 1) * P],
                                                   b["spt"][0:NSAMP, i % 2, 2, 8 * j:8 * j + 8], start=False, stop=True)
                        ins.then_inc(sem(f"spv_done_{tg}"), 1)

            def residual(p0, tiles, kn, tag, o_ready):
                eng.wait_ge(sem(o_ready), 1)
                per = tiles[1]
                for m in range(KD + 2):
                    if m < KD:
                        if m % per == 0:
                            take(0, p0 + m // per)
                        if m >= 4:
                            eng.wait_ge(sem(f"added_{tag}"), m - 3)
                        s = (p0 + m // per) % SPL
                        for k in range(kn):
                            c = (k * per + m % per) * P
                            ins = three(ps[m % 4][:, 0:T], whi[:, s, c:c + P], wlo[:, s, c:c + P], hh[:, k], hl[:, k],
                                        k == 0, k == kn - 1)
                        ins.then_inc(tile_sem(tiles, m), 1)
                    if m >= 2 and tag != "wob":
                        norm_sum("norm_f", m - 2)

            for k in range(KD):
                norm_sum("norm_a", k)
            project(A, tiles_a, lambda m: ("norm_a", hh, hl))
            to_tokens(A)
            prompt(A)
            sample(A, con("ident", A["rows"])[:, 0:A["hq"]])
            residual(P_WO, tiles_wo, KD, "wo", "o_split_a")

            for i in range(GU_P // 2):
                for part in range(2):
                    pc = P_GU + 2 * i + part
                    take(0, pc)
                    if i >= 2 and part == 0:
                        eng.wait_ge(sem("gated"), 2 * (i - 1))
                    for s in range(2):
                        bank = ps[4 * (i % 2) + 2 * part + s]
                        for k in range(KD):
                            if i == 0 and part == 0 and s == 0:
                                eng.wait_ge(sem("lo_ready_norm_f"), k + 1)
                            c = (k * 2 + s) * P
                            ins = three(bank[:, 0:T], whi[:, pc % SPL, c:c + P], wlo[:, pc % SPL, c:c + P], hh[:, k], hl[:, k],
                                        k == 0, k == KD - 1)
                        ins.then_inc(tile_sem(tiles_gu, 4 * i + 2 * part + s), 1)
            for m in range(KD + 2):
                if m < KD:
                    for part in range(2):
                        pc = P_DN + 2 * m + part
                        take(0, pc)
                        if m < 4 and part == 0:
                            if m == 0:
                                eng.wait_ge(sem("gated"), KF)
                        elif part == 0:
                            eng.wait_ge(sem("added_dn"), m - 3)
                        for k in range(11):
                            kk = 11 * part + k
                            if m == 0:
                                eng.wait_ge(sem("act_lo"), kk + 1)
                            ins = three(ps[m % 4][:, 0:T], whi[:, pc % SPL, k * P:(k + 1) * P], wlo[:, pc % SPL, k * P:(k + 1) * P],
                                        gh[:, kk], gl[:, kk], kk == 0, kk == KF - 1)
                        ins.then_inc(pieces_used, 1)
                if m >= 2:
                    norm_sum("norm_b", m - 2)

            project(B, tiles_b, lambda m: ("norm_b2", hh2, hl2) if 4 <= m < 16 else ("norm_b", hh, hl))
            to_tokens(B)
            prompt(B)
            sample(B, con("pick", B["rows"]))
            residual(P_WOB, tiles_wob, B["nj"], "wob", "o_split_b")

            n = 0
            for c, (t0, w) in enumerate(TB):
                for half in range(2):
                    if n == 0:
                        eng.wait_ge(sem("added_wob"), KD)
                    for u in range(4):
                        ins = nc.tensor.transpose(ps[n][0:w, u * P:(u + 1) * P], xT[:, 4 * half + u, t0:t0 + w], con("ident"))
                    ins.then_inc(sem("x_turned"), 1)
                    n += 1
            eng.wait_ge(sem("router_scaled"), 1)
            for c, (t0, w) in enumerate(TB):
                for k in range(KD):
                    ins = nc.tensor.matmul(ps[6][0:w, 8 * c:8 * c + 8], xT[:, k, t0:t0 + w], rwg[:, k], start=k == 0, stop=k == KD - 1)
            ins.then_inc(sem("routed"), 1)
            eng.wait_ge(sem("chosen"), 1)
            for c, (t0, w) in enumerate(TB):
                for d in range(c + 1):
                    wd = TB[d][1]
                    tri = con("before" if d == c else "ones", wd)[:, 0:w]
                    nc.tensor.matmul(ps[7][0:w, 8 * c:8 * c + 8], tri, sel[0:wd, 0, 8 * d:8 * d + 8], start=d == 0, stop=d == c)
            for d in range(3):
                wd = TB[d][1]
                ins = nc.tensor.matmul(ps[7][:, 32:40], con("ones", wd), sel[0:wd, 0, 8 * d:8 * d + 8], start=d == 0, stop=d == 2)
            ins.then_inc(sem("placed"), 1)

            def scatter(n):
                eng.wait_ge(sem("out_lo"), n + 1)
                for i in range(6):
                    c, half = i // 2, i % 2
                    w = TB[c][1]
                    if i < 3:
                        if i == 0:
                            eng.wait_ge(sem("gathered_lo"), 2 * n + 2)
                            eng.wait_ge(sem("pmt_copied"), n + 1)
                    else:
                        eng.wait_ge(sem("y_added"), 6 * n + i - 2)
                    for part, v in enumerate((oh, ol)):
                        ins = nc.tensor.matmul(ps[5 + i % 3][:, 0:512], pmt[:, c, :], v[:, 512 * half:512 * half + 512],
                                               start=part == 0, stop=part == 1)
                    ins.then_inc(sem("scattered"), 1)

            def one_hot_turn(n):
                eng.wait_ge(sem("y_added"), 6 * n + 6)
                for c, (t0, w) in enumerate(TB):
                    nc.tensor.transpose(ps[7][:, c * P:c * P + w], pm[0:w, c, :], con("ident", w)[:, 0:w])
                for c, (t0, w) in enumerate(TB):
                    ins = nc.tensor.matmul(ps[7][:, 384:385], pm[0:w, c, :], gcur[0:w, 0, c:c + 1], start=c == 0, stop=c == 2)
                ins.then_inc(sem("one_hot_turned"), 1)

            def gather(n):
                eng.wait_ge(sem("one_hot"), n + 1)
                for half in range(2):
                    for u in range(4):
                        k = 4 * half + u
                        for c, (t0, w) in enumerate(TB):
                            ins = nc.tensor.matmul(ps[5 + half][:, u * P:(u + 1) * P], htok[0:w, c, k * P:(k + 1) * P], pm[0:w, c, :],
                                                   start=c == 0, stop=c == 2)
                    ins.then_inc(sem("gathered"), 1)

            def expert(n):
                def turn(c):
                    eng.wait_ge(sem("act_ready"), 7 * n + c + 1)
                    if c > 0:
                        eng.wait_ge(sem("actl_ready"), 7 * n + c)
                    for u in range(4):
                        ins = nc.tensor.transpose(ps[4][:, u * P:(u + 1) * P], am[:, u * P:(u + 1) * P], con("ident"))
                    ins.then_inc(sem("act_turned"), 1)

                for c in range(7):
                    for part in range(2):
                        if part == 0 and c > 0:
                            eng.wait_ge(sem("silu_done"), 7 * n + c)
                        if part == 1 and c > 0:
                            eng.wait_ge(sem("act_ready"), 7 * n + c)
                        for half in range(2):
                            q = 4 * c + 2 * part + half
                            take(n, PRE + q)
                            if q == 0:
                                eng.wait_ge(sem("gathered_lo"), 2 * n + 2)
                            for k in range(4):
                                kk = 4 * half + k
                                w = slice(k * 512, (k + 1) * 512)
                                ins = three(ps[part][:, :], xgh[:, kk], xgl[:, kk], whi[:, q % SPL, w], wlo[:, q % SPL, w],
                                            kk == 0, kk == KD - 1)
                            ins.then_inc(pieces_used, 1)
                        if part == 0 and c >= 1:
                            turn(c - 1)
                        if c == 1 and part == 0:
                            scatter(n)
                        if c == 2 and part == 0:
                            one_hot_turn(n)
                for dq in range(EXP_DN):
                    q = EXP_GU + dq
                    take(n, PRE + q)
                    if dq == 0:
                        eng.wait_ge(sem("out_scaled"), 2 * n + 2)
                    if dq == 1:
                        turn(6)
                    for k in range(2):
                        kk = 2 * dq + k
                        if kk % 4 == 0:
                            eng.wait_ge(sem("actl_ready"), 7 * n + kk // 4 + 1)
                        for half in range(2):
                            w = slice(k * D + 512 * half, k * D + 512 * half + 512)
                            ins = three(ps[2 + half][:, :], acth[:, kk], actl[:, kk], whi[:, q % SPL, w], wlo[:, q % SPL, w],
                                        kk == 0, kk == KE - 1)
                    ins.then_inc(pieces_used, 1)
                    if dq == 3:
                        gather(n + 1)

            gather(0)
            with eng.Fori(0, NE) as n:
                expert(n)
            eng.wait_ge(sem("table_ready"), 1)
            over = eng.value_load(tab[0:1, 12:13], min_val=0, max_val=4)
            with eng.Fori(0, 4) as t:
                with eng.If(t < over):
                    expert(t + NE)
            scatter(over + NE)

        @block.scalar
        def _(eng):
            eng.wait_ge(sem("const_loaded"), 16)
            done = [0]

            def split_upto(p):
                while done[0] <= min(p, PRE - 1):
                    src = W[done[0]]
                    split_hi(eng, 0, done[0], src.shape[1] * src.shape[2])
                    done[0] += 1

            eps = con("eps")

            def square(tag, k, add_tag=None):
                if add_tag:
                    eng.wait_ge(sem(f"added_{add_tag}"), k + 1)
                nc.scalar.activation(sq[:, k], xT[:, k], ACT.Square).then_inc(sem(f"squared_{tag}"), 1)

            def norm_root(tag):
                eng.wait_ge(sem(f"summed_{tag}"), 1)
                nc.scalar.activation(rt[:, 0], ps[7][:, 0:T], ACT.Sqrt, bias=eps).then_inc(sem(f"root_{tag}"), 1)

            def norm_hi(tag, dst):
                for k in range(KD):
                    eng.wait_ge(sem(f"hn_{tag}"), k + 1)
                    nc.scalar.activation(dst[:, k], hn[:, k], ACT.Copy).then_inc(sem(f"hi_{tag}"), 1)

            def project(b, tiles):
                nrot, nt = b["nrot"], b["nrot"] + b["nv"]
                for m in range(nt):
                    if m % 2 == 0:
                        split_upto(b["pieces"] + m // 2 + 2)
                    if m < nrot:
                        eng.wait_ge(tile_sem(tiles, m), tile_count(tiles, m))
                        if m >= 2:
                            eng.wait_ge(sem(f"head_summed_{b['tag']}"), m - 1)
                        nc.scalar.activation(sq[:, m % 2], ps[m % 4][:, 0:T], ACT.Square).then_inc(sem(f"tile_squared_{b['tag']}"), 1)
                    else:
                        eng.wait_ge(tile_sem(tiles, m), tile_count(tiles, m))
                        nc.scalar.activation(b["vT"][:, m - nrot], ps[m % 4][:, 0:T], ACT.Copy).then_inc(sem(f"v_copied_{b['tag']}"), 1)
                    if 0 <= m - 1 < nrot:
                        r = m - 1
                        eng.wait_ge(sem(f"head_summed_{b['tag']}"), r + 1)
                        if r >= 2:
                            eng.wait_ge(sem(f"scaled_{b['tag']}"), r - 1)
                        nc.scalar.activation(rt[:, r % 2], ps[4 + r % 2][:, 0:T], ACT.Sqrt, bias=eps).then_inc(sem(f"rooted_{b['tag']}"), 1)

            def prompt(b):
                tg = b["tag"]
                for h in range(b["nh"] + 3):
                    if 0 <= h - 2 < b["nh"]:
                        i = h - 2
                        eng.wait_ge(sem(f"pt_turned_{tg}"), i + 1)
                        if i >= 2:
                            eng.wait_ge(sem(f"pv_done_{tg}"), i - 1)
                        nc.scalar.activation(b["pt"][:, i % 2, :], ps[6][:, 0:384], ACT.Copy).then_inc(sem(f"pt_copied_{tg}"), 1)
                    if h < b["nh"]:
                        eng.wait_ge(sem(f"maxed_{tg}"), h + 1)
                        for i, (lo, hi) in enumerate(((0, P), (P, 384))):
                            ins = nc.scalar.activation(b["p"][:, h % 2, :, lo:hi], b["s"][:, h % 2, :, lo:hi], ACT.Exp,
                                                       bias=b["st"][:, h % 2, 2 + i:3 + i], accum_out=b["st"][:, h % 2, 4 + i:5 + i])
                            ins.then_inc(sem(f"exped_{tg}"), 1)
                    if 0 <= h - 3 and (h - 3) % 2 == 1:
                        i = h - 3
                        eng.wait_ge(sem(f"pv_done_{tg}"), i + 1)
                        nc.scalar.activation(b["oT"][:, i // 2, 0:SEQ], ps[7][:, 0:SEQ], ACT.Copy).then_inc(sem(f"o_copied_{tg}"), 1)

            def sample(b):
                tg, half = b["tag"], b["nj"] // 2
                for q in range(NSEQ + 2):
                    if q < NSEQ:
                        for c in range(0, half, 2):
                            n = q * half + c
                            eng.wait_ge(sem(f"ktr_done_{tg}"), n + 1)
                            if q >= 1:
                                eng.wait_ge(sem(f"sscored_{tg}"), q)
                            nc.scalar.activation(b["keys"][:, 2 * c:2 * c + 2, 0:PAST], ps[n % 4][:, :].rearrange("p (j n) -> p j n", j=2),
                                                 ACT.Copy).then_inc(sem(f"keys_copied0_{tg}"), 1)
                    if 0 <= q - 2:
                        i = q - 2
                        eng.wait_ge(sem(f"spt_turned_{tg}"), i + 1)
                        if i >= 2:
                            eng.wait_ge(sem(f"spv_done_{tg}"), i - 1)
                        nc.scalar.activation(b["spt"][:, i % 2, 0:2, :], ps[6][:, 0:2 * b["hq"]].rearrange("p (c n) -> p c n", c=2), ACT.Copy)
                        nc.scalar.activation(b["spt"][0:NSAMP, i % 2, 2, :], ps[6][0:NSAMP, 2 * b["hq"]:3 * b["hq"]], ACT.Copy)\
                            .then_inc(sem(f"spt_copied_{tg}"), 1)
                    if 0 <= q - 1 < NSEQ:
                        i = q - 1
                        eng.wait_ge(sem(f"smaxed_{tg}"), i + 1)
                        if i >= 2:
                            eng.wait_ge(sem(f"spt_turned_{tg}"), i - 1)
                        nc.scalar.activation(b["sp"][:, i % 2, :], b["ss"][:, i % 2, :], ACT.Exp, bias=b["sst"][:, i % 2, 1:2],
                                             accum_out=b["sst"][:, i % 2, 2:3]).then_inc(sem(f"sexped_{tg}"), 1)

            def o_hi(b):
                eng.wait_ge(sem(f"so_copied_{b['tag']}"), NSEQ)
                nc.scalar.activation(hh[:, 0:b["nj"]], b["oT"][:, :, :], ACT.Copy).then_inc(sem(f"o_hi_{b['tag']}"), 1)

            eng.wait_ge(sem("x_loaded"), 16)
            for k in range(KD):
                square("norm_a", k)
            split_upto(1)
            norm_root("norm_a")
            norm_hi("norm_a", hh)
            project(A, tiles_a)
            prompt(A)
            sample(A)
            o_hi(A)
            for m in range(KD):
                if m % 2 == 0:
                    split_upto(P_WO + m // 2 + 2)
                square("norm_f", m, "wo")
            norm_root("norm_f")
            norm_hi("norm_f", hh)
            for i in range(GU_P // 2 + 1):
                if i < GU_P // 2:
                    split_upto(P_GU + 2 * i + 2)
                    for s in range(2):
                        t = 2 * i + s
                        eng.wait_ge(tile_sem(tiles_gu, 4 * i + s), tile_count(tiles_gu, 4 * i + s))
                        if t >= 4:
                            eng.wait_ge(sem("gated"), t - 3)
                        nc.scalar.activation(gate_s[:, t % 4], ps[4 * (i % 2) + s][:, 0:T], ACT.Silu).then_inc(sem("silued"), 1)
                    split_upto(P_GU + 2 * i + 3)
                if i >= 1:
                    for s in range(2):
                        t = 2 * (i - 1) + s
                        eng.wait_ge(sem("gated"), t + 1)
                        nc.scalar.activation(gh[:, t], gate_u[:, t % 4], ACT.Copy).then_inc(sem("act_hi"), 1)
            for m in range(KD):
                split_upto(P_DN + 2 * m + 3)
                square("norm_b", m, "dn")
            norm_root("norm_b")
            norm_hi("norm_b", hh)
            norm_hi("norm_b2", hh2)
            project(B, tiles_b)
            prompt(B)
            sample(B)
            o_hi(B)
            split_upto(PRE - 1)
            for c, (t0, w) in enumerate(TB):
                eng.wait_ge(sem("x_rows"), 2 * c + 2)
                nc.scalar.activation(htok[0:w, c, :], xtok[0:w, c, :], ACT.Square, accum_out=mst[0:w, c, 0:1]).then_inc(sem("row_squared"), 1)
            eng.wait_ge(sem("mst_ready"), 1)
            eng.wait_ge(sem("row_squared"), 3)
            nc.scalar.activation(mst[:, :, 1], mst[:, :, 0], ACT.Sqrt, bias=eps, scale=1.0 / D).then_inc(sem("row_root"), 1)
            eng.wait_ge(sem("gap_ready"), 1)
            nc.scalar.activation(mst[:, :, 4], mst[:, :, 3], ACT.Exp).then_inc(sem("gap_exp"), 1)
            split_hi(eng, 0, PRE)
            split_hi(eng, 0, PRE + 1)

            def gather_hi(n):
                for half in range(2):
                    eng.wait_ge(sem("gathered"), 2 * n + half + 1)
                    nc.scalar.activation(xgh[:, 4 * half:4 * half + 4, :].rearrange("p k n -> p (k n)"), ps[5 + half][:, :], ACT.Copy)\
                        .then_inc(sem("gathered_hi"), 1)

            def expert(n):
                def quad_hi(c):
                    eng.wait_ge(sem("act_turned"), 7 * n + c + 1)
                    nc.scalar.activation(acth[:, 4 * c:4 * c + 4, :].rearrange("p k n -> p (k n)"), ps[4][:, :], ACT.Copy)\
                        .then_inc(sem("acth_ready"), 1)

                for q in range(PER):
                    split_hi(eng, n, PRE + q + 2)
                    if q < EXP_GU:
                        c, r = q // 4, q % 4
                        if r == 1:
                            eng.wait_ge(pieces_used, PER * n + PRE + q + 1)
                            if c >= 1:
                                eng.wait_ge(sem("act_ready"), 7 * n + c)
                            nc.scalar.activation(sg[:, :], ps[0][:, :], ACT.Silu).then_inc(sem("silu_done"), 1)
                            if c >= 1:
                                quad_hi(c - 1)
                        if q == 2:
                            eng.wait_ge(sem("out_scaled"), 2 * n + 2)
                            nc.scalar.activation(oh[:, :], oe[:, :], ACT.Copy).then_inc(sem("out_hi"), 1)
                        if q == 10:
                            eng.wait_ge(sem("one_hot_turned"), n + 1)
                            nc.scalar.activation(pmt[:, 0:2, :].rearrange("p c n -> p (c n)"), ps[7][:, 0:2 * P], ACT.Copy)
                            nc.scalar.activation(pmt[:, 2, 0:NSAMP], ps[7][:, 2 * P:2 * P + NSAMP], ACT.Copy)
                            nc.scalar.activation(gsl[:, 0:1], ps[7][:, 384:385], ACT.Copy).then_inc(sem("pmt_copied"), 1)
                    else:
                        if q == EXP_GU + 1:
                            quad_hi(6)
                        if q == EXP_GU + 4:
                            gather_hi(n + 1)
                eng.wait_ge(pieces_used, PER * n + PRE + PER)
                eng.wait_ge(sem("out_lo"), n + 1)
                eng.wait_ge(sem("pmt_copied"), n + 2)
                for half in range(2):
                    nc.scalar.activation(oe[:, 512 * half:512 * half + 512], ps[2 + half][:, :], ACT.Copy, scale=gsl[:, 0:1])\
                        .then_inc(sem("out_scaled"), 1)

            gather_hi(0)
            with eng.Fori(0, NE) as n:
                expert(n)
            eng.wait_ge(sem("table_ready"), 1)
            over = eng.value_load(tab[0:1, 12:13], min_val=0, max_val=4)
            with eng.Fori(0, 4) as t:
                with eng.If(t < over):
                    expert(t + NE)
            last = over + NE
            eng.wait_ge(sem("out_scaled"), 2 * last + 2)
            nc.scalar.activation(oh[:, :], oe[:, :], ACT.Copy).then_inc(sem("out_hi"), 1)

        @block.vector
        def _(eng):
            eng.wait_ge(sem("const_loaded"), 16)
            done = [0]

            def split_upto(p):
                while done[0] <= min(p, PRE - 1):
                    src = W[done[0]]
                    split_lo(eng, 0, done[0], src.shape[1] * src.shape[2])
                    done[0] += 1

            steps = [0]

            def chain(ins):
                steps[0] += 1
                ins.then_inc(sem("vector_step"), 1)
                eng.wait_ge(sem("vector_step"), steps[0])

            V = nc.vector

            def norm(tag, src_tag, name, dst, dsl):
                if src_tag:
                    eng.wait_ge(sem(f"root_{src_tag}"), 1)
                    chain(V.reciprocal(rs[:, 0], rt[:, 0]))
                else:
                    eng.wait_ge(sem("lo_ready_norm_b"), KD)
                for k in range(KD):
                    V.scalar_tensor_tensor(out=hn[:, k], in0=xT[:, k], scalar=gain(name, k), in1=rs[:, 0], op0=ALU.mult,
                                           op1=ALU.mult).then_inc(sem(f"hn_{tag}"), 1)
                for k in range(KD):
                    eng.wait_ge(sem(f"hi_{tag}"), k + 1)
                    V.tensor_tensor(dsl[:, k], hn[:, k], dst[:, k].bitcast(F32), ALU.subtract).then_inc(sem(f"lo_ready_{tag}"), 1)

            def project(b, tiles, gains, dest):
                nrot, nt = b["nrot"], b["nrot"] + b["nv"]
                for m in range(nt + 1):
                    if m < nt and m % 2 == 0:
                        split_upto(b["pieces"] + m // 2 + 2)
                    if 0 <= m - 2 < nrot:
                        r = m - 2
                        eng.wait_ge(sem(f"turned_{b['tag']}"), r + 1)
                        dst = dest(r)
                        chain(V.tensor_tensor(sq[:, 4 + r % 2], ps[6 + r % 2][:, 0:T], con("sin"), ALU.mult))
                        chain(V.tensor_tensor(dst, sq[:, 2 + r % 2], con("cos"), ALU.mult))
                        V.tensor_tensor(dst, dst, sq[:, 4 + r % 2], ALU.add).then_inc(sem(f"rotated_{b['tag']}"), 1)
                        eng.wait_ge(sem(f"rotated_{b['tag']}"), r + 1)
                    if 0 <= m - 1 < nrot:
                        r = m - 1
                        eng.wait_ge(sem(f"rooted_{b['tag']}"), r + 1)
                        chain(V.reciprocal(rs[:, r % 2], rt[:, r % 2]))
                        V.scalar_tensor_tensor(out=sq[:, 2 + r % 2], in0=ps[r % 4][:, 0:T], scalar=gain(gains(r), 0), in1=rs[:, r % 2],
                                               op0=ALU.mult, op1=ALU.mult).then_inc(sem(f"scaled_{b['tag']}"), 1)
                        eng.wait_ge(sem(f"scaled_{b['tag']}"), r + 1)

            def to_tokens(b):
                for i in range(2 * b["nj"]):
                    dst = b["ktok"] if i < b["nj"] else b["vtok"]
                    j = i % b["nj"]
                    eng.wait_ge(sem(f"tok_turned_{b['tag']}"), i + 1)
                    V.tensor_copy(dst[:, 0:2, j * P:(j + 1) * P], ps[i % 4][:, 0:2 * P].rearrange("p (c n) -> p c n", c=2))
                    V.tensor_copy(dst[0:NSAMP, 2, j * P:(j + 1) * P], ps[i % 4][0:NSAMP, 2 * P:3 * P]).then_inc(sem(f"tok_done_{b['tag']}"), 1)

            def prompt(b):
                tg = b["tag"]
                eng.wait_ge(sem(f"mask_loaded_{tg}"), 16)
                eng.wait_ge(sem(f"kv_stored_{tg}"), 64)
                for h in range(b["nh"] + 1):
                    if h < b["nh"]:
                        eng.wait_ge(sem(f"scored_{tg}"), h + 1)
                        if h >= 2:
                            eng.wait_ge(sem(f"exped_{tg}"), 2 * (h - 1))
                        st = b["st"][:, h % 2]
                        for g in range(b["ng"]):
                            ins = V.scalar_tensor_tensor(out=b["s"][:, h % 2, g], in0=ps[(h % 2) * b["ng"] + g][:, 0:384], scalar=SCALE,
                                                         in1=b["mask"][:, 384 * g:384 * (g + 1)], op0=ALU.mult, op1=ALU.add)
                        ins.then_inc(sem(f"masked_{tg}"), 1)
                        eng.wait_ge(sem(f"masked_{tg}"), h + 1)
                        V.tensor_reduce(st[:, 0:1], b["s"][:, h % 2, :, 0:P], AXXY, ALU.max)
                        chain(V.tensor_reduce(st[:, 1:2], b["s"][:, h % 2, :, P:384], AXXY, ALU.max))
                        V.tensor_scalar(st[:, 2:4], st[:, 0:2], -1.0, None, ALU.mult).then_inc(sem(f"maxed_{tg}"), 1)
                    if h >= 1:
                        i = h - 1
                        st = b["st"][:, i % 2]
                        eng.wait_ge(sem(f"exped_{tg}"), 2 * (i + 1))
                        chain(V.reciprocal(st[:, 6:8], st[:, 4:6]))
                        for g in range(1, b["ng"]):
                            chain(V.tensor_tensor(b["p"][:, i % 2, 0], b["p"][:, i % 2, 0], b["p"][:, i % 2, g], ALU.add))
                        V.tensor_scalar(b["p"][:, i % 2, 0, 0:P], b["p"][:, i % 2, 0, 0:P], st[:, 6:7], None, ALU.mult)
                        V.tensor_scalar(b["p"][:, i % 2, 0, P:384], b["p"][:, i % 2, 0, P:384], st[:, 7:8], None, ALU.mult)\
                            .then_inc(sem(f"probs_{tg}"), 1)

            def sample(b):
                tg, half, hq = b["tag"], b["nj"] // 2, b["hq"]
                chain(V.memset(b["qblk"][:, :, :, :].rearrange("p a j n -> p (a j n)"), 0.0))
                chain(V.tensor_copy(b["keys"][:, :, PAST:PAST + NSAMP], b["kT"][:, :, SEQ:T]))

                def join(st, op):
                    for g in range(b["ng"]):
                        ins = V.tensor_copy(st[0:hq, 4 + g:5 + g], st[g * hq:(g + 1) * hq, 3:4])
                    chain(ins)
                    chain(V.tensor_reduce(st[0:hq, 8:9], st[0:hq, 4:4 + b["ng"]], AXX, op))
                    for g in range(b["ng"]):
                        ins = V.tensor_copy(st[g * hq:(g + 1) * hq, 3:4], st[0:hq, 8:9])
                    chain(ins)

                for q in range(NSEQ + 2):
                    if q < NSEQ:
                        if q >= 2:
                            eng.wait_ge(sem(f"sscored_{tg}"), q - 1)
                        for g in range(b["ng"]):
                            for j in range(b["nj"]):
                                for r in range(2):
                                    c = g * hq + (2 * j + r) * QLEN
                                    ins = V.tensor_copy(b["qblk"][64 * r:64 * r + 64, q % 2, j, c:c + QLEN],
                                                        b["qT"][64 * r:64 * r + 64, g * b["nj"] + j, SEQ + QLEN * q:SEQ + QLEN * (q + 1)])
                        ins.then_inc(sem(f"qblk_{tg}"), 1)
                        for c in range(1, half, 2):
                            n = q * half + c
                            eng.wait_ge(sem(f"ktr_done_{tg}"), n + 1)
                            if q >= 1:
                                eng.wait_ge(sem(f"sscored_{tg}"), q)
                            V.tensor_copy(b["keys"][:, 2 * c:2 * c + 2, 0:PAST], ps[n % 4][:, :].rearrange("p (j n) -> p j n", j=2))\
                                .then_inc(sem(f"keys_copied1_{tg}"), 1)
                    if 0 <= q - 2:
                        i = q - 2
                        eng.wait_ge(sem(f"spv_done_{tg}"), i + 1)
                        t0 = SEQ + QLEN * i
                        o8 = ps[7][:, 0:8 * b["nj"]].rearrange("p (j c) -> p j c", c=8)
                        V.tensor_copy(b["oT"][0:64, :, t0:t0 + QLEN], o8[0:64, :, 0:QLEN])
                        V.tensor_copy(b["oT"][64:P, :, t0:t0 + QLEN], o8[64:P, :, QLEN:2 * QLEN]).then_inc(sem(f"so_copied_{tg}"), 1)
                    if 0 <= q - 1 < NSEQ:
                        i = q - 1
                        st, s, bank = b["sst"][:, i % 2], b["ss"][:, i % 2], ps[4 + i % 2]
                        eng.wait_ge(sem(f"sscored_{tg}"), i + 1)
                        m0 = 384 * b["ng"]
                        if b["ng"] > 1:
                            V.scalar_tensor_tensor(out=s[:, 0:PAST], in0=bank[0:b["rows"], 0:PAST], scalar=SCALE,
                                                   in1=b["mask"][0:b["rows"], m0:m0 + PAST], op0=ALU.mult, op1=ALU.add)
                            m0 += PAST
                        else:
                            V.tensor_scalar(s[:, 0:PAST], bank[0:b["rows"], 0:PAST], SCALE, None, ALU.mult)
                        m0 += NSAMP * i
                        V.scalar_tensor_tensor(out=s[:, PAST:PAST + NSAMP], in0=bank[0:b["rows"], PAST:PAST + NSAMP], scalar=SCALE,
                                               in1=b["mask"][0:b["rows"], m0:m0 + NSAMP], op0=ALU.mult, op1=ALU.add).then_inc(sem(f"smasked_{tg}"), 1)
                        eng.wait_ge(sem(f"smasked_{tg}"), i + 1)
                        chain(V.tensor_reduce(st[:, 3:4], s, AXX, ALU.max))
                        if b["ng"] > 1:
                            join(st, ALU.max)
                        V.tensor_scalar(st[:, 1:2], st[:, 3:4], -1.0, None, ALU.mult).then_inc(sem(f"smaxed_{tg}"), 1)
                        eng.wait_ge(sem(f"sexped_{tg}"), i + 1)
                        if b["ng"] > 1:
                            chain(V.tensor_copy(st[:, 3:4], st[:, 2:3]))
                            join(st, ALU.add)
                            chain(V.reciprocal(st[:, 9:10], st[:, 3:4]))
                        else:
                            chain(V.reciprocal(st[:, 9:10], st[:, 2:3]))
                        V.tensor_scalar(b["sp"][:, i % 2], b["sp"][:, i % 2], st[:, 9:10], None, ALU.mult).then_inc(sem(f"sprobs_{tg}"), 1)

            def o_lo(b):
                eng.wait_ge(sem(f"o_hi_{b['tag']}"), 1)
                V.tensor_tensor(hl[:, 0:b["nj"]], b["oT"][:, :, :], hh[:, 0:b["nj"]].bitcast(F32), ALU.subtract).then_inc(sem(f"o_split_{b['tag']}"), 1)

            def add_tile(m, tag):
                V.tensor_tensor(xT[:, m], xT[:, m], ps[m % 4][:, 0:T], ALU.add).then_inc(sem(f"added_{tag}"), 1)

            eng.wait_ge(sem("x_loaded"), 16)
            split_upto(1)
            norm("norm_a", "norm_a", "g_attn_a", hh, hl)
            project(A, tiles_a, lambda r: "qn_a" if r < 8 else "kn_a", lambda r: A["qT"][:, r] if r < 8 else A["kT"][:, r - 8])
            to_tokens(A)
            prompt(A)
            sample(A)
            o_lo(A)
            for m in range(KD):
                if m % 2 == 0:
                    split_upto(P_WO + m // 2 + 2)
                eng.wait_ge(tile_sem(tiles_wo, m), tile_count(tiles_wo, m))
                add_tile(m, "wo")
            norm("norm_f", "norm_f", "g_ffn0", hh, hl)
            for i in range(GU_P // 2 + 1):
                if i < GU_P // 2:
                    split_upto(P_GU + 2 * i + 3)
                    for s in range(2):
                        t = 2 * i + s
                        eng.wait_ge(sem("silued"), t + 1)
                        eng.wait_ge(tile_sem(tiles_gu, 4 * i + 2 + s), tile_count(tiles_gu, 4 * i + 2 + s))
                        if t >= 4:
                            eng.wait_ge(sem("act_lo"), t - 3)
                        V.tensor_tensor(gate_u[:, t % 4], gate_s[:, t % 4], ps[4 * (i % 2) + 2 + s][:, 0:T], ALU.mult).then_inc(sem("gated"), 1)
                if i >= 1:
                    for s in range(2):
                        t = 2 * (i - 1) + s
                        eng.wait_ge(sem("act_hi"), t + 1)
                        V.tensor_tensor(gl[:, t], gate_u[:, t % 4], gh[:, t].bitcast(F32), ALU.subtract).then_inc(sem("act_lo"), 1)
            for m in range(KD):
                split_upto(P_DN + 2 * m + 3)
                eng.wait_ge(pieces_used, P_DN + 2 * m + 2)
                add_tile(m, "dn")
            norm("norm_b", "norm_b", "g_kv", hh, hl)
            norm("norm_b2", None, "g_attn_b", hh2, hl2)
            project(B, tiles_b, lambda r: "kn_b" if r < 4 else "qn_b", lambda r: B["kT"][:, r] if r < 4 else B["qT"][:, r - 4])
            to_tokens(B)
            prompt(B)
            sample(B)
            o_lo(B)
            split_upto(PRE - 1)
            for m in range(KD):
                eng.wait_ge(tile_sem(tiles_wob, m), tile_count(tiles_wob, m))
                add_tile(m, "wob")

            eng.wait_ge(sem("router_loaded"), 32)
            g1 = CONST["g_ffn1"][0]
            for k in range(KD):
                ins = V.tensor_scalar(rwg[:, k], rw[:, k], cst[:, g1 + k:g1 + k + 1], None, ALU.mult)
            ins.then_inc(sem("router_scaled"), 1)
            chain(V.memset(mst[:, :, :], 1.0))
            V.memset(sel[:, :, :], 0.0).then_inc(sem("mst_ready"), 1)
            n = 0
            for c, (t0, w) in enumerate(TB):
                for half in range(2):
                    eng.wait_ge(sem("x_turned"), n + 1)
                    V.tensor_copy(xtok[0:w, c, 512 * half:512 * half + 512], ps[n][0:w, :]).then_inc(sem("x_rows"), 1)
                    n += 1
            eng.wait_ge(sem("row_root"), 1)
            chain(V.reciprocal(mst[:, :, 2], mst[:, :, 1]))
            for c, (t0, w) in enumerate(TB):
                ins = V.scalar_tensor_tensor(out=htok[0:w, c, :], in0=xtok[0:w, c, :], scalar=mst[0:w, c, 2:3], in1=grow[0:w, :],
                                             op0=ALU.mult, op1=ALU.mult)
            chain(ins)
            eng.wait_ge(sem("routed"), 1)
            eng.wait_ge(sem("mst_ready"), 1)

            def s3(i, rows=P):
                return sel[0:rows, i, :].rearrange("p (c e) -> p c e", e=NE)

            def bc(col):
                return mst[:, :, col:col + 1].to_broadcast([P, 3, NE])

            for c, (t0, w) in enumerate(TB):
                ins = V.tensor_scalar(sel[0:w, 1, 8 * c:8 * c + 8], ps[6][0:w, 8 * c:8 * c + 8], mst[0:w, c, 2:3], None, ALU.mult)
            chain(ins)
            iota = con("expert").rearrange("p (c e) -> p c e", e=NE)

            def first_max(src, top, onehot):
                chain(V.tensor_reduce(mst[:, :, top], s3(src), AXX, ALU.max))
                chain(V.tensor_tensor(s3(2), s3(src), bc(top), ALU.is_ge))
                chain(V.tensor_scalar(s3(3), s3(2), -64.0, 64.0, ALU.mult, ALU.add))
                chain(V.tensor_tensor(s3(3), s3(3), iota, ALU.add))
                chain(V.tensor_reduce(mst[:, :, 7], s3(3), AXX, ALU.min))
                chain(V.tensor_tensor(s3(onehot), iota, bc(7), ALU.is_equal))

            first_max(1, 5, 4)
            chain(V.tensor_scalar(s3(6), s3(4), 3.0e38, None, ALU.mult))
            chain(V.tensor_tensor(s3(7), s3(1), s3(6), ALU.subtract))
            first_max(7, 6, 5)
            V.tensor_tensor(mst[:, :, 3], mst[:, :, 6], mst[:, :, 5], ALU.subtract).then_inc(sem("gap_ready"), 1)
            chain(V.tensor_tensor(s3(8), s3(4), s3(5), ALU.add))
            V.tensor_copy(sel[:, 0, 0:16], sel[:, 8, 0:16])
            V.tensor_copy(sel[0:NSAMP, 0, 16:24], sel[0:NSAMP, 8, 16:24]).then_inc(sem("chosen"), 1)
            eng.wait_ge(sem("gap_exp"), 1)
            chain(V.tensor_scalar(mst[:, :, 5], mst[:, :, 4], 1.0, None, ALU.add))
            chain(V.reciprocal(mst[:, :, 6], mst[:, :, 5]))
            chain(V.tensor_tensor(mst[:, :, 7], mst[:, :, 6], mst[:, :, 4], ALU.mult))
            chain(V.tensor_tensor(s3(2), s3(4), bc(6), ALU.mult))
            chain(V.tensor_tensor(s3(3), s3(5), bc(7), ALU.mult))
            chain(V.tensor_tensor(s3(9), s3(2), s3(3), ALU.add))
            eng.wait_ge(sem("chosen"), 1)
            eng.wait_ge(sem("placed"), 1)
            for c, (t0, w) in enumerate(TB):
                ins = V.tensor_scalar(sel[0:w, 10, 8 * c:8 * c + 8], ps[7][0:w, 8 * c:8 * c + 8], 1.0, None, ALU.add)
            chain(ins)
            chain(V.tensor_tensor(s3(10), s3(10), s3(0), ALU.mult))
            chain(V.tensor_scalar(s3(10), s3(10), -1.0, None, ALU.add))
            chain(V.memset(pslot[:, :, :], -1.0))
            chain(V.memset(gslot[:, :, :], 0.0))
            chain(V.tensor_copy(pslot[:, :, 0:NE], s3(10)))
            chain(V.tensor_copy(gslot[:, :, 0:NE], s3(9)))

            def one_hot(n):
                V.tensor_copy(pcur[:, :], pslot[:, :, bass.ds(n, 1)].rearrange("p c o -> p (c o)")).then_inc(sem("places_copied"), 1)
                eng.wait_ge(sem("places_copied"), n + 1)
                for c, (t0, w) in enumerate(TB):
                    ins = V.tensor_scalar(pm[0:w, c, :], con("slots", w), pcur[0:w, c:c + 1], None, ALU.is_equal)
                ins.then_inc(sem("one_hot"), 1)

            def gather_lo(n):
                for half in range(2):
                    eng.wait_ge(sem("gathered_hi"), 2 * n + half + 1)
                    V.tensor_tensor(xgl[:, 4 * half:4 * half + 4, :].rearrange("p k n -> p (k n)"), ps[5 + half][:, :],
                                    xgh[:, 4 * half:4 * half + 4, :].bitcast(F32).rearrange("p k n -> p (k n)"), ALU.subtract)\
                        .then_inc(sem("gathered_lo"), 1)

            def out_lo(n):
                eng.wait_ge(sem("out_hi"), n + 1)
                V.tensor_tensor(ol[:, :], oe[:, :], oh[:, :].bitcast(F32), ALU.subtract).then_inc(sem("out_lo"), 1)

            def add_rows(n):
                for i in range(6):
                    c, half = i // 2, i % 2
                    w = TB[c][1]
                    eng.wait_ge(sem("scattered"), 6 * n + i + 1)
                    y = xtok[0:w, c, 512 * half:512 * half + 512]
                    V.tensor_tensor(y, y, ps[5 + i % 3][0:w, :], ALU.add).then_inc(sem("y_added"), 1)

            chain(V.memset(oe[:, :], 0.0))
            chain(V.memset(pmt[:, :, :].bitcast(F32), 0.0))
            V.memset(gsl[:, :], 0.0).then_inc(sem("out_scaled"), 2)
            eng.wait_ge(sem("out_scaled"), 2)
            one_hot(0)
            split_lo(eng, 0, PRE)
            split_lo(eng, 0, PRE + 1)
            gather_lo(0)
            ov = lambda i: ovf[:, i, :]
            ovb = CONST["over"][0]
            ov_e, ov_b = cst[:, ovb:ovb + 16], cst[:, ovb + 16:ovb + 32]
            cnt = ps[7][:, 32:40].unsqueeze(2).to_broadcast([P, NE, 2])
            chain(V.tensor_tensor(ov(0).rearrange("p (e b) -> p e b", b=2), cnt, ov_b.rearrange("p (e b) -> p e b", b=2), ALU.is_gt))
            chain(V.memset(ov(1), 1.0))
            chain(V.tensor_tensor_scan(ov(2), ov(1), ov(0), 0.0, ALU.mult, ALU.add))
            chain(V.memset(tabf[:, :], 0.0))
            chain(V.tensor_reduce(tabf[:, 12:13], ov(0), AXX, ALU.add))
            for j in range(4):
                chain(V.tensor_scalar(ov(3), ov(2), float(j + 1), None, ALU.is_equal))
                chain(V.tensor_tensor(ov(3), ov(3), ov(0), ALU.mult))
                chain(V.tensor_tensor(ov(4), ov(3), ov_e, ALU.mult))
                chain(V.tensor_reduce(tabf[:, 8 + j:9 + j], ov(4), AXX, ALU.add))
                chain(V.tensor_tensor(ov(4), ov(3), ov_b, ALU.mult))
                chain(V.tensor_reduce(tabf[:, 13:14], ov(4), AXX, ALU.add))
                chain(V.tensor_reduce(ov(5)[:, 0:8], ov(3).rearrange("p (e b) -> p e b", b=2), AXX, ALU.add))
                pick = ov(5)[:, 0:8].unsqueeze(1).to_broadcast([P, 3, NE])
                chain(V.tensor_scalar(s3(3), s3(10), 1.0, None, ALU.add))
                chain(V.tensor_tensor(s3(2), s3(3), pick, ALU.mult))
                chain(V.tensor_reduce(mst[:, :, 0], s3(2), AXX, ALU.add))
                chain(V.tensor_scalar(pslot[:, :, 8 + j], mst[:, :, 0], -1.0, tabf[:, 13:14], ALU.add, ALU.subtract))
                chain(V.tensor_tensor(s3(2), s3(9), pick, ALU.mult))
                chain(V.tensor_reduce(gslot[:, :, 8 + j], s3(2), AXX, ALU.add))
            V.tensor_copy(tab[:, :], tabf[:, :]).then_inc(sem("table_ready"), 1)

            V.memset(scratch[:, 1:2], 0.0).then_inc(sem("pmt_copied"), 1)

            def expert(n):
                def quad_lo(c):
                    eng.wait_ge(sem("acth_ready"), 7 * n + c + 1)
                    V.tensor_tensor(actl[:, 4 * c:4 * c + 4, :].rearrange("p k n -> p (k n)"), ps[4][:, :],
                                    acth[:, 4 * c:4 * c + 4, :].bitcast(F32).rearrange("p k n -> p (k n)"), ALU.subtract)\
                        .then_inc(sem("actl_ready"), 1)

                for q in range(PER):
                    split_lo(eng, n, PRE + q + 2)
                    if q < EXP_GU:
                        c, r = q // 4, q % 4
                        if r == 3:
                            eng.wait_ge(sem("silu_done"), 7 * n + c + 1)
                            eng.wait_ge(pieces_used, PER * n + PRE + q + 1)
                            V.tensor_tensor(am[:, :], sg[:, :], ps[1][:, :], ALU.mult).then_inc(sem("act_ready"), 1)
                        if r == 1 and c >= 1:
                            quad_lo(c - 1)
                        if q == 2:
                            out_lo(n)
                        if q == 5:
                            V.tensor_copy(gcur[:, 0, :], gslot[:, :, bass.ds(n, 1)].rearrange("p c o -> p (c o)"))
                            add_rows(n)
                    else:
                        if q == EXP_GU + 1:
                            quad_lo(6)
                            eng.wait_ge(sem("one_hot_turned"), n + 1)
                            one_hot(n + 1)
                        if q == EXP_GU + 4:
                            gather_lo(n + 1)

            with eng.Fori(0, NE) as n:
                expert(n)
            eng.wait_ge(sem("table_ready"), 1)
            over = eng.value_load(tab[0:1, 12:13], min_val=0, max_val=4)
            with eng.Fori(0, 4) as t:
                with eng.If(t < over):
                    expert(t + NE)
            last = over + NE
            out_lo(last)
            add_rows(last)
            V.memset(scratch[:, 2:3], 0.0).then_inc(sem("y_ready"), 1)


def constants():
    import numpy as np
    c = np.zeros((P, NCONST), np.float32)

    def put(name, a):
        lo, hi = CONST[name]
        c[:, lo:hi] = a

    i = np.arange(P)
    put("ident", np.eye(P))
    put("headsum", (i[:, None] // DH == i[None, :] // DH) / DH)
    put("featsum", np.full((P, P), 1.0 / D))
    half = DH // 8
    rot = np.zeros((P, P))
    cos, sin = np.ones((P, T), np.float32), np.zeros((P, T), np.float32)
    inv = (500000.0 ** (-2.0 * np.arange(half, dtype=np.float32) / (2 * half))).astype(np.float32)
    pos = np.concatenate([np.arange(SEQ), np.tile(PAST + np.arange(QLEN), NSEQ)]).astype(np.float32)
    ang = (pos[None, :] * inv[:, None]).astype(np.float32)
    for h in range(0, P, DH):
        for d in range(half):
            rot[h + half + d, h + d] = -1.0
            rot[h + d, h + half + d] = 1.0
        for o in (0, half):
            cos[h + o:h + o + half] = np.cos(ang)
            sin[h + o:h + o + half] = np.sin(ang)
    put("rot", rot)
    put("cos", cos)
    put("sin", sin)
    put("before", i[:, None] < i[None, :])
    put("ones", 1.0)
    put("slots", i[None, :] * np.ones((P, 1)))
    put("pick", i[:, None] % NSAMP == np.arange(NSAMP)[None, :])
    put("expert", np.tile(np.arange(NE), 3)[None, :] * np.ones((P, 1)))
    over = np.concatenate([np.repeat(np.arange(NE), 2), np.tile([128.0, 256.0], NE)])
    put("over", over[None, :] * np.ones((P, 1)))
    put("eps", EPS)
    return c


def masks():
    import numpy as np
    i = np.arange(P)

    def prompt(ok):
        t = np.arange(SEQ)
        m = ok(t[:, None], t[None, :])
        return np.concatenate([m[0:P, 0:P], m[P:, :]], axis=1)

    def sample(ok, ng_rows):
        rows = i[:ng_rows] % QLEN
        past = ok(PAST + rows[:, None], np.arange(PAST)[None, :])
        new = np.zeros((ng_rows, NSEQ, NSEQ, QLEN), bool)
        for s in range(NSEQ):
            new[:, s, s] = ok(PAST + rows[:, None], PAST + np.arange(QLEN)[None, :])
        return past, new.reshape(ng_rows, -1)

    causal = lambda q, k: k <= q
    ma = np.zeros((P, MASK_A), bool)
    ma[:, 0:384] = prompt(causal)
    ma[0:HA * QLEN, 384:] = sample(causal, HA * QLEN)[1]
    mb = np.zeros((P, MASK_B), bool)
    for g, (win, dil) in enumerate(((128, 1), (512, 4), (2048, 16))):
        ok = lambda q, k: (k <= q) & (q - k <= win) & ((q - k) % dil == 0)
        mb[:, 384 * g:384 * (g + 1)] = prompt(ok)
        n = HB * QLEN
        past, new = sample(ok, n)
        mb[g * n:(g + 1) * n, 384 * GB:384 * GB + PAST] = past
        mb[g * n:(g + 1) * n, 384 * GB + PAST:] = new
    return tuple(np.where(m, 0.0, NEG).astype(np.float32) for m in (ma, mb))


def kernel(x_prompt, x_sample, cache_a_k, cache_a_v, cache_b_k, cache_b_v, page_table,
           norm_attn_a, w_qkv_a, qnorm_a, knorm_a, w_o_a,
           norm_kv_b, w_kv_b, knorm_b, norm_attn_b, w_q_b, qnorm_b, w_o_b,
           norm_ffn, w_gu_dense, w_down_dense, w_router, w_gu_moe, w_down_moe):
    import numpy as np
    import concourse.bacc as bacc
    from concourse.bass_utils import run_bass_kernel_spmd

    nc = bacc.Bacc("TRN2", target_bir_lowering=False, num_devices=1)
    x = np.concatenate([np.asarray(x_prompt).reshape(SEQ, D), np.asarray(x_sample).reshape(NSAMP, D)], axis=0)
    const = constants()
    for name, v in (("g_attn_a", norm_attn_a), ("g_ffn0", norm_ffn[0]), ("g_kv", norm_kv_b), ("g_attn_b", norm_attn_b),
                    ("g_ffn1", norm_ffn[1])):
        lo, hi = CONST[name]
        const[:, lo:hi] = np.asarray(v).reshape(KD, P).T
    for name, v in (("qn_a", qnorm_a), ("kn_a", knorm_a), ("qn_b", qnorm_b), ("kn_b", knorm_b)):
        lo, hi = CONST[name]
        const[:, lo] = np.tile(np.asarray(v).reshape(DH), 2)
    mask_a, mask_b = masks()
    arrays = dict(
        g_rows=np.tile(np.asarray(norm_ffn)[1].reshape(1, D), (P, 1)),
        xT=np.ascontiguousarray(x.reshape(T, KD, P).transpose(2, 1, 0)), const=const, mask_a=mask_a, mask_b=mask_b,
        cache_a_k=np.asarray(cache_a_k).reshape(1, NPHYS, PAGE, HA * DH), cache_a_v=np.asarray(cache_a_v).reshape(1, NPHYS, PAGE, HA * DH),
        cache_b_k=np.asarray(cache_b_k).reshape(NSEQ, PAST, HB * DH), cache_b_v=np.asarray(cache_b_v).reshape(NSEQ, PAST, HB * DH),
        page_table=np.asarray(page_table).reshape(1, 2 * NSEQ), w_qkv_a=w_qkv_a, w_o_a=w_o_a, w_kv_b=w_kv_b, w_q_b=w_q_b,
        w_o_b=w_o_b, w_gu_dense=w_gu_dense, w_down_dense=w_down_dense, w_router=w_router, w_gu_moe=w_gu_moe,
        w_down_moe=w_down_moe)
    arrays = {f"in_{k}": np.ascontiguousarray(v) for k, v in arrays.items()}
    io = {k[3:]: nc.dram_tensor(k, v.shape, mybir.dt.from_np(v.dtype), kind="ExternalInput").ap() for k, v in arrays.items()}
    for name, width in (("y", D), ("ak", HA * DH), ("av", HA * DH), ("bk", HB * DH), ("bv", HB * DH)):
        io[name] = nc.dram_tensor(f"out_{name}", (T, width), F32, kind="ExternalOutput").ap()
    build_program(nc, io)
    got = run_bass_kernel_spmd(nc, [arrays], core_ids=[0]).results[0]
    y, ak, av, bk, bv = (got[f"out_{n}"] for n in ("y", "ak", "av", "bk", "bv"))
    return (y[:SEQ].reshape(1, SEQ, D), y[SEQ:].reshape(NSEQ, QLEN, D),
            ak[:SEQ].reshape(1, 1, SEQ, HA, DH), av[:SEQ].reshape(1, 1, SEQ, HA, DH),
            bk[:SEQ].reshape(1, SEQ, HB, DH), bv[:SEQ].reshape(1, SEQ, HB, DH),
            ak[SEQ:].reshape(1, NSEQ, QLEN, HA, DH), av[SEQ:].reshape(1, NSEQ, QLEN, HA, DH),
            bk[SEQ:].reshape(NSEQ, QLEN, HB, DH), bv[SEQ:].reshape(NSEQ, QLEN, HB, DH))
```
